# Optimizing a Trainium2 kernel written in Bass

```python
import jax, jax.numpy as jnp
from jax import lax
import numpy as np
import math

D_MODEL = 1024
BATCH = 1
SEQ = 512
DEPTH = 2

N_A = DEPTH // 2
N_B = DEPTH - N_A
HEAD_DIM = 64
MEM_LEN = 256
N_MEM_HEADS = 4
MEM_WIDTH = N_MEM_HEADS * HEAD_DIM
MIX_WIDTH = D_MODEL - MEM_WIDTH
CONV_CH = MIX_WIDTH
CONV_WIDTH = 31
N_FOX_HEADS = MIX_WIDTH // HEAD_DIM
D_FF = 2816
FFN_CONV_WIDTH = 3
BLOCK_Q = 128
RMS_EPS = 1e-6
LN_EPS = 1e-5


def rmsnorm(x, g):
    xf = x.astype(jnp.float32)
    y = xf * lax.rsqrt(jnp.mean(xf * xf, axis=-1, keepdims=True) + RMS_EPS)
    return (y * g.astype(jnp.float32)).astype(x.dtype)

def layernorm(x, g, b):
    xf = x.astype(jnp.float32)
    mu = jnp.mean(xf, axis=-1, keepdims=True)
    var = jnp.mean(jnp.square(xf - mu), axis=-1, keepdims=True)
    y = (xf - mu) * lax.rsqrt(var + LN_EPS)
    return (y * g.astype(jnp.float32) + b.astype(jnp.float32)).astype(x.dtype)

def causal_dwconv(x, w, b):
    width, ch = w.shape
    y = lax.conv_general_dilated(
        x, w[:, None, :].astype(x.dtype), window_strides=(1,),
        padding=((width - 1, 0),), dimension_numbers=("NWC", "WIO", "NWC"),
        feature_group_count=ch)
    return y + b

def conformer_conv(u, b_glu, w_dw, b_dw, ln_g, ln_b):
    u = u + b_glu
    a, gate = jnp.split(u, 2, axis=-1)
    v = a * jax.nn.sigmoid(gate)
    v = causal_dwconv(v, w_dw, b_dw)
    v = layernorm(v, ln_g, ln_b)
    return jax.nn.silu(v)

def memory_attention(q, mem_k, mem_v):
    b, s, _ = q.shape
    qh = q.reshape(b, s, N_MEM_HEADS, HEAD_DIM)
    kh = mem_k.reshape(b, -1, N_MEM_HEADS, HEAD_DIM)
    vh = mem_v.reshape(b, -1, N_MEM_HEADS, HEAD_DIM)
    logits = jnp.einsum("bshd,bmhd->bhsm", qh, kh).astype(jnp.float32) * (HEAD_DIM ** -0.5)
    p = jax.nn.softmax(logits, axis=-1).astype(vh.dtype)
    o = jnp.einsum("bhsm,bmhd->bshd", p, vh)
    return o.reshape(b, s, MEM_WIDTH)

def forgetting_attention(q, k, v, cum_logf):
    b, s, h, dh = q.shape
    scale = dh ** -0.5
    outs = []
    for i in range(s // BLOCK_Q):
        q0 = i * BLOCK_Q
        kend = q0 + BLOCK_Q
        qb = q[:, q0:kend]
        kb = k[:, :kend]
        vb = v[:, :kend]
        logits = jnp.einsum("bqhd,bkhd->bhqk", qb, kb).astype(jnp.float32) * scale
        logits = logits + cum_logf[:, :, q0:kend, None] - cum_logf[:, :, None, :kend]
        qpos = q0 + jnp.arange(BLOCK_Q)
        kpos = jnp.arange(kend)
        logits = jnp.where(kpos[None, :] <= qpos[:, None], logits, -jnp.inf)
        p = jax.nn.softmax(logits, axis=-1).astype(vb.dtype)
        outs.append(jnp.einsum("bhqk,bkhd->bqhd", p, vb))
    return jnp.concatenate(outs, axis=1)

def conv_ffn(h, w_up, w_dw, b_dw, w_down):
    u = h @ w_up
    u = causal_dwconv(u, w_dw, b_dw)
    gate, val = jnp.split(u, 2, axis=-1)
    return (jax.nn.silu(gate) * val) @ w_down

def first_inputs(seed: int = 0) -> dict:
    key = jax.random.key(seed)
    ks = jax.random.split(key, 24)
    f32 = jnp.float32
    nrm = lambda k, shape, scale: jax.random.normal(k, shape, f32) * scale
    gain = lambda k, shape: 1.0 + 0.05 * jax.random.normal(k, shape, f32)
    d = D_MODEL
    return {
        "x": jax.random.normal(ks[0], (BATCH, SEQ, d), f32),
        "mem": jax.random.normal(ks[1], (BATCH, MEM_LEN, d), f32),
        "g_mix": gain(ks[2], (DEPTH, d)),
        "w_in_a": nrm(ks[3], (N_A, d, 2 * CONV_CH + MEM_WIDTH), d ** -0.5),
        "b_glu": nrm(ks[4], (N_A, 2 * CONV_CH), 0.02),
        "w_dw_a": nrm(ks[5], (N_A, CONV_WIDTH, CONV_CH), CONV_WIDTH ** -0.5),
        "b_dw_a": nrm(ks[6], (N_A, CONV_CH), 0.02),
        "ln_g": gain(ks[7], (N_A, CONV_CH)),
        "ln_b": nrm(ks[8], (N_A, CONV_CH), 0.02),
        "g_kv": gain(ks[9], (d,)),
        "w_kvf": nrm(ks[10], (d, 2 * MIX_WIDTH + N_FOX_HEADS), d ** -0.5),
        "b_f": 2.0 + 0.5 * jax.random.normal(ks[11], (N_FOX_HEADS,), f32),
        "w_in_b": nrm(ks[12], (N_B, d, MIX_WIDTH + MEM_WIDTH), d ** -0.5),
        "g_mem": gain(ks[13], (d,)),
        "w_mem_kv": nrm(ks[14], (DEPTH, d, 2 * MEM_WIDTH), d ** -0.5),
        "w_out": nrm(ks[15], (DEPTH, d, d), d ** -0.5),
        "g_ffn": gain(ks[16], (DEPTH, d)),
        "w_up": nrm(ks[17], (DEPTH, d, 2 * D_FF), d ** -0.5),
        "w_dw_f": nrm(ks[18], (DEPTH, FFN_CONV_WIDTH, 2 * D_FF), FFN_CONV_WIDTH ** -0.5),
        "b_dw_f": nrm(ks[19], (DEPTH, 2 * D_FF), 0.02),
        "w_down": nrm(ks[20], (DEPTH, D_FF, d), D_FF ** -0.5),
        "g_final": gain(ks[21], (d,)),
    }

def first_block(x, mem, g_mix, w_in_a, b_glu, w_dw_a, b_dw_a, ln_g, ln_b, g_kv, w_kvf, b_f,
              w_in_b, g_mem, w_mem_kv, w_out, g_ffn, w_up, w_dw_f, b_dw_f, w_down, g_final):
    bsz, seq, _ = x.shape
    mem_n = rmsnorm(mem, g_mem)
    k_sh = v_sh = cum_logf = None
    for l in range(DEPTH):
        h = rmsnorm(x, g_mix[l])
        mem_k, mem_v = jnp.split(mem_n @ w_mem_kv[l], 2, axis=-1)
        if l < N_A:
            p = h @ w_in_a[l]
            u, q_mem = p[..., :2 * CONV_CH], p[..., 2 * CONV_CH:]
            mix = conformer_conv(u, b_glu[l], w_dw_a[l], b_dw_a[l], ln_g[l], ln_b[l])
        else:
            if l == N_A:
                hk = rmsnorm(x, g_kv)
                kvf = hk @ w_kvf
                k_sh = kvf[..., :MIX_WIDTH].reshape(bsz, seq, N_FOX_HEADS, HEAD_DIM)
                v_sh = kvf[..., MIX_WIDTH:2 * MIX_WIDTH].reshape(bsz, seq, N_FOX_HEADS, HEAD_DIM)
                f_logit = (kvf[..., 2 * MIX_WIDTH:] + b_f).astype(jnp.float32)
                cum_logf = jnp.cumsum(jax.nn.log_sigmoid(f_logit), axis=1).transpose(0, 2, 1)
            p = h @ w_in_b[l - N_A]
            q, q_mem = p[..., :MIX_WIDTH], p[..., MIX_WIDTH:]
            q = q.reshape(bsz, seq, N_FOX_HEADS, HEAD_DIM)
            mix = forgetting_attention(q, k_sh, v_sh, cum_logf).reshape(bsz, seq, MIX_WIDTH)
        mem_o = memory_attention(q_mem, mem_k, mem_v)
        x = x + jnp.concatenate([mix, mem_o], axis=-1) @ w_out[l]
        x = x + conv_ffn(rmsnorm(x, g_ffn[l]), w_up[l], w_dw_f[l], b_dw_f[l], w_down[l])
    return rmsnorm(x, g_final)


GRID_W = 64
CHUNK = 128
Q_BLOCK = 128
D_A = D_MODEL // 2
H_A = 8
HD_A = D_A // H_A
D_B = D_MODEL // 2
H_B = D_B // HEAD_DIM
KV_HEADS = 2
Q_PER_KV = H_B // KV_HEADS
D_KV = KV_HEADS * HEAD_DIM
ROPE_AXIS_DIM = HEAD_DIM // 2
ROPE_THETA = 10000.0
EPS = 1e-6
SPLITS = (D_A, D_A, D_A, D_B, D_KV, D_KV, D_B)
D_IN = sum(SPLITS)
D_MIX = D_A + D_B


def rmsnorm_2(x, g):
    xf = x.astype(jnp.float32)
    y = xf * lax.rsqrt(jnp.mean(xf * xf, axis=-1, keepdims=True) + EPS)
    return (y * g.astype(jnp.float32)).astype(x.dtype)

def layernorm_2(x, g, b):
    xf = x.astype(jnp.float32)
    mu = jnp.mean(xf, axis=-1, keepdims=True)
    var = jnp.mean(jnp.square(xf - mu), axis=-1, keepdims=True)
    y = (xf - mu) * lax.rsqrt(var + EPS)
    return (y * g.astype(jnp.float32) + b.astype(jnp.float32)).astype(x.dtype)

def axial_rope_tables(seq_len):
    rows = seq_len // GRID_W
    row = jnp.broadcast_to(jnp.arange(rows, dtype=jnp.float32)[:, None], (rows, GRID_W)).reshape(-1)
    col = jnp.broadcast_to(jnp.arange(GRID_W, dtype=jnp.float32)[None, :], (rows, GRID_W)).reshape(-1)
    inv = ROPE_THETA ** (-jnp.arange(0, ROPE_AXIS_DIM, 2, dtype=jnp.float32) / ROPE_AXIS_DIM)
    ang_r = row[:, None] * inv[None, :]
    ang_c = col[:, None] * inv[None, :]
    return jnp.cos(ang_r), jnp.sin(ang_r), jnp.cos(ang_c), jnp.sin(ang_c)

def _rot_half(x, cos, sin):
    n = x.shape[-1] // 2
    c = cos[:, None, :].astype(x.dtype)
    s = sin[:, None, :].astype(x.dtype)
    x1, x2 = x[..., :n], x[..., n:]
    return jnp.concatenate([x1 * c - x2 * s, x2 * c + x1 * s], axis=-1)

def apply_axial_rope(x, tables):
    cr, sr, cc, sc = tables
    xr = _rot_half(x[..., :ROPE_AXIS_DIM], cr, sr)
    xc = _rot_half(x[..., ROPE_AXIS_DIM:], cc, sc)
    return jnp.concatenate([xr, xc], axis=-1)

def gmlp_group(u, v, ln_g, ln_b, ws, sb):
    b, s, _ = v.shape
    nc = s // CHUNK
    vn = layernorm_2(v, ln_g, ln_b).reshape(b, nc, CHUNK, H_A, HD_A)
    z = jnp.einsum('hij,bcjhd->bcihd', ws, vn) + sb.T[None, None, :, :, None]
    return u * z.reshape(b, s, D_A)

def gqa_axial_attention(q, k, v, qn_g, kn_g, tables):
    b, s, _ = q.shape
    q = rmsnorm_2(q.reshape(b, s, H_B, HEAD_DIM), qn_g)
    k = rmsnorm_2(k.reshape(b, s, KV_HEADS, HEAD_DIM), kn_g)
    v = v.reshape(b, s, KV_HEADS, HEAD_DIM)
    q = apply_axial_rope(q, tables)
    k = apply_axial_rope(k, tables)
    scale = HEAD_DIM ** -0.5
    nb = s // Q_BLOCK
    qb = q.reshape(b, nb, Q_BLOCK, KV_HEADS, Q_PER_KV, HEAD_DIM).transpose(1, 0, 2, 3, 4, 5)

    def attend(qblk):
        sc = jnp.einsum('bqkgd,bskd->bkgqs', qblk, k).astype(jnp.float32) * scale
        p = jax.nn.softmax(sc, axis=-1).astype(v.dtype)
        return jnp.einsum('bkgqs,bskd->bqkgd', p, v)

    o = lax.map(attend, qb)
    return o.transpose(1, 0, 2, 3, 4, 5).reshape(b, s, D_B)

def second_inputs(seed: int = 0) -> dict:
    key = jax.random.key(seed)
    ks = jax.random.split(key, 12)
    f32 = jnp.float32
    x = jax.random.normal(ks[0], (BATCH, SEQ, D_MODEL), f32)
    w_in = jax.random.normal(ks[1], (DEPTH, D_MODEL, D_IN), f32) * D_MODEL ** -0.5
    w_out = jax.random.normal(ks[2], (DEPTH, D_MIX, D_MODEL), f32) * D_MIX ** -0.5
    pre_g = 1.0 + 0.05 * jax.random.normal(ks[3], (DEPTH, D_MODEL), f32)
    post_g = 1.0 + 0.05 * jax.random.normal(ks[4], (DEPTH, D_MODEL), f32)
    ln_a_g = 1.0 + 0.05 * jax.random.normal(ks[5], (DEPTH, D_A), f32)
    ln_a_b = 0.02 * jax.random.normal(ks[6], (DEPTH, D_A), f32)
    spatial_w = jax.random.normal(ks[7], (DEPTH, H_A, CHUNK, CHUNK), f32) * CHUNK ** -0.5
    spatial_b = 1.0 + 0.05 * jax.random.normal(ks[8], (DEPTH, H_A, CHUNK), f32)
    q_norm_g = 1.0 + 0.05 * jax.random.normal(ks[9], (DEPTH, HEAD_DIM), f32)
    k_norm_g = 1.0 + 0.05 * jax.random.normal(ks[10], (DEPTH, HEAD_DIM), f32)
    return {"x": x, "w_in": w_in, "w_out": w_out, "pre_g": pre_g, "post_g": post_g,
            "ln_a_g": ln_a_g, "ln_a_b": ln_a_b, "spatial_w": spatial_w, "spatial_b": spatial_b,
            "q_norm_g": q_norm_g, "k_norm_g": k_norm_g}

def second_block(x, w_in, w_out, pre_g, post_g, ln_a_g, ln_a_b, spatial_w, spatial_b, q_norm_g, k_norm_g):
    seq_len = x.shape[1]
    tables = axial_rope_tables(seq_len)
    idx = list(np.cumsum(SPLITS)[:-1])
    for l in range(DEPTH):
        h = rmsnorm_2(x, pre_g[l])
        proj = jnp.einsum('bsd,de->bse', h, w_in[l])
        u_a, v_a, g_a, q, k, v, g_b = jnp.split(proj, idx, axis=-1)
        y_a = gmlp_group(u_a, v_a, ln_a_g[l], ln_a_b[l], spatial_w[l], spatial_b[l]) * jax.nn.silu(g_a)
        y_b = gqa_axial_attention(q, k, v, q_norm_g[l], k_norm_g[l], tables) * jax.nn.silu(g_b)
        y = jnp.concatenate([y_a, y_b], axis=-1)
        out = jnp.einsum('bse,ed->bsd', y, w_out[l])
        x = x + rmsnorm_2(out, post_g[l])
    return x


def setup_inputs(seed=0):
    out = dict(first_inputs(seed))
    for name, value in second_inputs(seed + 1).items():
        if name != "x":
            out[name + "_2"] = value
    return out


def reference(
    x, mem, g_mix, w_in_a, b_glu, w_dw_a, b_dw_a, ln_g, ln_b, g_kv, w_kvf, b_f, w_in_b, g_mem,
    w_mem_kv, w_out, g_ffn, w_up, w_dw_f, b_dw_f, w_down, g_final, w_in_2, w_out_2, pre_g_2,
    post_g_2, ln_a_g_2, ln_a_b_2, spatial_w_2, spatial_b_2, q_norm_g_2, k_norm_g_2,
):
    x = first_block(
        x, mem, g_mix, w_in_a, b_glu, w_dw_a, b_dw_a, ln_g, ln_b, g_kv, w_kvf, b_f, w_in_b,
        g_mem, w_mem_kv, w_out, g_ffn, w_up, w_dw_f, b_dw_f, w_down, g_final,
    )
    return second_block(
        x, w_in_2, w_out_2, pre_g_2, post_g_2, ln_a_g_2, ln_a_b_2, spatial_w_2, spatial_b_2,
        q_norm_g_2, k_norm_g_2,
    )


_drawn_inputs = setup_inputs


def setup_inputs(seed=0):
    import zlib

    import numpy as np

    out = dict(_drawn_inputs(seed))
    spreads = {}
    factors = {'ln_b': 2.724, 'g_mem': 6.029, 'ln_a_b_2': 3.948, 'q_norm_g_2': 8.0, 'k_norm_g_2': 8.0}
    for name, (base, spread) in spreads.items():
        noise = np.random.default_rng([zlib.crc32(name.encode()), seed]).standard_normal(out[name].shape)
        drawn = base * np.exp(spread * noise) if base else spread * noise
        out[name] = __import__('jax').numpy.asarray(drawn.astype(out[name].dtype))
    for name, factor in factors.items():
        out[name] = (out[name] * factor).astype(out[name].dtype)
    return out
```

```python
from contextlib import ExitStack

import concourse.bass as bass
from concourse import mybir

P = 128
T = 512
TM = 256
D = 1024
KT = D // P
HD = 64
MIX = 768
MT = MIX // P
CW = 31
DFF = 2816
FT = DFF // P
QT = T // P
UNIT = KT * P
SLOTS = 4
AHEAD = SLOTS - 1
N_FOX = 12
N_MEM = 4
N_GQA = 8
DA = 512
AT = DA // P
RMS_EPS = 1e-6
LN_EPS = 1e-5
EPS_2 = 1e-6
NEG = -1e30

UP_UNITS = 2 * FT
DOWN_PER_TILE = 3
DOWN_UNITS = DOWN_PER_TILE * KT
U_GLU = 0
U_QM0 = U_GLU + 2 * MT
U_MEM = U_QM0 + 2
U_OUT0 = U_MEM + 8
U_UP0 = U_OUT0 + KT
U_DN0 = U_UP0 + UP_UNITS
U_KVF = U_DN0 + DOWN_UNITS
U_Q = U_KVF + 2 * MT + 1
U_OUT1 = U_Q + KT
U_UP1 = U_OUT1 + KT
U_DN1 = U_UP1 + UP_UNITS
U_IN2 = U_DN1 + DOWN_UNITS
IN2_UNITS = DFF // P
L2_UNITS = IN2_UNITS + KT
UNITS = U_IN2 + 2 * L2_UNITS


def accs_before(u):
    n = u
    for first in (U_DN0, U_DN1):
        inside = min(max(u - first, 0), DOWN_UNITS)
        n -= inside - inside // DOWN_PER_TILE
    return n


PARAMS = {}


def _place_params():
    at = 0
    for name, n in (("g_mix0", KT), ("g_mix1", KT), ("b_glu", 2 * MT), ("w_dw_a", MT * CW), ("b_dw_a", MT),
                    ("ln_g", MT), ("ln_b", MT), ("g_kv", KT), ("b_f", 1), ("g_mem", KT), ("g_ffn0", KT),
                    ("g_ffn1", KT), ("w_dw_f0", 2 * FT * 3), ("w_dw_f1", 2 * FT * 3), ("b_dw_f0", 2 * FT),
                    ("b_dw_f1", 2 * FT), ("g_final", KT), ("pre_g0", KT), ("pre_g1", KT), ("post_g0", KT),
                    ("post_g1", KT), ("lna_g0", AT), ("lna_g1", AT), ("lna_b0", AT), ("lna_b1", AT),
                    ("qn0", 1), ("qn1", 1), ("kn0", 1), ("kn1", 1)):
        PARAMS[name] = at
        at += n
    return at


N_PARAMS = _place_params()


class Tally:

    def __init__(self, sem, engine):
        self.sem, self.engine, self.n, self.at = sem, engine, 0, 0

    def did(self, ins):
        self.n += 1
        ins.then_inc(self.sem, 1)
        return ins

    def wait(self):
        self.engine.wait_ge(self.sem, self.at + self.n)

    def link(self, ins):
        self.did(ins)
        self.wait()


def two_blocks(nc, wstream, xT, memT, params, consts, rope, wsT, sbT, out):
    f32, f32r, bf16 = mybir.dt.float32, mybir.dt.float32r, mybir.dt.bfloat16
    ALU = mybir.AluOpType
    ACT = mybir.ActivationFunctionType
    AX = mybir.AxisListType
    MUL, ADD, SUB = ALU.mult, ALU.add, ALU.subtract

    ctx = ExitStack()
    with ctx:
        start = (nc.sbuf_base + 31) // 32 * 32
        cursor = [start]

        def put(name, shape, dt, at=None):
            size = 4 if dt != bf16 else 2
            for n in shape[1:]:
                size *= n
            size = (size + 31) // 32 * 32
            where = cursor[0] if at is None else at
            if at is None:
                cursor[0] += size
            return nc.alloc_sbuf_tensor_at(name, shape, dt, offset=where)

        x = put("x", [P, KT, T], f32)
        xs_hi = put("xs_hi", [P, KT, T], f32r)
        xs_lo = put("xs_lo", [P, KT, T], f32r)
        raw = [put(f"raw{s}", [P, UNIT], f32) for s in range(SLOTS)]
        w_hi = [put(f"w_hi{s}", [P, KT, P], f32r) for s in range(SLOTS)]
        w_lo = [put(f"w_lo{s}", [P, KT, P], f32r) for s in range(SLOTS)]
        fs_at = cursor[0]
        cursor[0] += 4 * (T + 8) * 4
        u_g = put("u_g", [P, T + 2], f32, fs_at)
        u_v = put("u_v", [P, T + 2], f32, fs_at + (T + 8) * 4)
        t_g = put("t_g", [P, T], f32, fs_at + 2 * (T + 8) * 4)
        t_v = put("t_v", [P, T], f32, fs_at + 3 * (T + 8) * 4)
        prob = [put(f"prob{i}", [P, T], f32, fs_at + i * T * 4) for i in range(3)]
        sq = [t_g, t_v]
        chan_sum = put("chan_sum", [P, T], f32, fs_at)
        rstd_ln = put("rstd_ln", [P, T], f32, fs_at + (T + 8) * 4)
        rstd = put("rstd", [P, T], f32)
        sq_sum = put("sq_sum", [P, T], f32)
        mem_kv1 = put("mem_kv1", [P, 4, TM], f32)
        small = put("small", [P, 64], f32)
        small_r = put("small_r", [P, 64], f32)
        nmax = put("nmax", [P, 4], f32)
        rsum = put("rsum", [P, 4], f32)
        rinv = put("rinv", [P, 4], f32)
        cst = put("cst", [P, 4 * P + 2], f32)
        par = put("par", [P, N_PARAMS], f32)
        ident_b = put("ident_b", [P, P], bf16)
        mask_b = put("mask_b", [P, P], bf16)
        h0 = cursor[0]

        def region():
            at = [h0]

            def take(name, shape, dt=f32):
                n = 4
                for m in shape[1:]:
                    n *= m
                t = put(name, shape, dt, at[0])
                at[0] += (n + 31) // 32 * 32
                assert at[0] <= h0 + 2 * FT * T * 4
                return t
            return take

        assert h0 + 2 * FT * T * 4 <= nc.sbuf_usable_end, (h0 + 2 * FT * T * 4, nc.sbuf_usable_end)
        ident, ones, rotm = cst[:, 0:P], cst[:, P:2 * P], cst[:, 2 * P:3 * P]
        mask = cst[:, 3 * P:4 * P]
        headsel = cst[:, 4 * P:4 * P + 2]

        def col(name, k=0):
            return par[:, PARAMS[name] + k:PARAMS[name] + k + 1]

        take = region()
        hid_hi = take("hid_hi", [P, FT, T], f32r)
        hid_lo = take("hid_lo", [P, FT, T], f32r)
        take = region()
        memx = take("memx", [P, KT, TM])
        mem_hi = take("mem_hi", [P, KT, TM], f32r)
        mem_lo = take("mem_lo", [P, KT, TM], f32r)
        glu = take("glu", [P, MT, T + CW - 1])
        conv = take("conv", [P, MT, T])
        qm0 = take("qm0", [P, 2, T])
        mem_kv0 = take("mem_kv0", [P, 4, TM])
        vm0 = take("vm0", [P, 2, TM])
        pt0 = [take(f"pt0_{i}", [P, 2, T]) for i in range(2)]
        sqm = [take(f"sqm{i}", [P, TM]) for i in range(2)]
        sqm_sum = take("sqm_sum", [P, TM])
        rstd_m = take("rstd_m", [P, TM])
        gate = take("gate", [P, T])
        take = region()
        qf = take("qf", [P, MT, T])
        kf = take("kf", [P, MT, T])
        vst = [take(f"vst{i}", [P, T]) for i in range(2)]
        vf = take("vf", [P, QT, MIX])
        qm1 = take("qm1", [P, 2, T])
        vm1 = take("vm1", [P, 2, TM])
        pt1 = [take(f"pt1_{i}", [P, QT, T]) for i in range(2)]
        fl = [take(f"fl{i}", [P, T]) for i in range(4)]
        take = region()
        qk = take("qk", [P, 5, T])
        vch = take("vch", [P, T])
        vtok = take("vtok", [P, QT, P])
        va = take("va", [P, AT, T])
        ua = take("ua", [P, AT, T])
        ga = [take(f"ga{i}", [P, T]) for i in range(2)]
        gb = take("gb", [P, AT, T])
        va_tok = take("va_tok", [P, QT, DA])
        sq_qk = take("sq_qk", [P, 5, T])
        ws_sb = take("ws_sb", [P, N_GQA, P])
        sb_sb = take("sb_sb", [P, AT, P])
        rope_sb = take("rope_sb", [P, 2, T])
        roped = take("roped", [P, T])
        pt2 = [take(f"pt2_{i}", [P, QT, T]) for i in range(2)]

        def o_sb(m):
            return pt2[m // QT][:, m % QT, :]

        bank = [ctx.enter_context(nc.psum_tensor(f"bank{i}", [P, T], f32)) for i in range(8)]
        acc = bank[0:2]
        b_stat, b_cast = bank[2], bank[3]
        b_s = [bank[0], bank[1], bank[4], bank[5]]
        b_t = bank[6:8]
        b_o = bank[2:4]
        b_vt = [bank[6], bank[7]]

        def sem(name):
            return ctx.enter_context(nc.semaphore(name))

        consts_in = sem("consts_in")
        params_in = sem("params_in")
        x_in = [sem("x_in0"), sem("x_in1")]
        mem_in = sem("mem_in")
        l2_in = sem("l2_in")
        unit_in = [sem(f"unit_in{s}") for s in range(SLOTS)]
        unit_hi = sem("unit_hi")
        unit_lo = sem("unit_lo")
        unit_used = sem("unit_used")
        acc_free = sem("acc_free")
        consts_b = sem("consts_b")
        split_hi = sem("split_hi")
        split_lo = sem("split_lo")
        squared = sem("squared")
        sq_added = sem("sq_added")
        stat_up = sem("stat_up")
        stat_inv = sem("stat_inv")
        stat_root = sem("stat_root")
        cast_up = sem("cast_up")
        cast_down = sem("cast_down")
        x_new = sem("x_new")
        sum_up = sem("sum_up")
        dve_did = sem("dve_did")
        act_did = sem("act_did")
        memsplit_hi = sem("memsplit_hi")
        memsplit_lo = sem("memsplit_lo")
        a_gate = sem("a_gate")
        s_sum = sem("s_sum")
        s_norm = sem("s_norm")
        s_act = sem("s_act")
        s_cent = sem("s_cent")
        vt_up = sem("vt_up")
        vt_down = sem("vt_down")
        at_s = sem("at_s")
        at_max = sem("at_max")
        at_exp = sem("at_exp")
        at_inv = sem("at_inv")
        at_p = sem("at_p")
        at_t = sem("at_t")
        at_pt = sem("at_pt")
        at_o = sem("at_o")
        f_act = sem("f_act")
        f_done = sem("f_done")
        tap_mid = sem("tap_mid")
        tap0 = sem("tap0")
        taps = sem("taps")
        silu_g = sem("silu_g")
        h_mul = sem("h_mul")
        h_hi = sem("h_hi")
        h_lo = sem("h_lo")
        q_sq = sem("q_sq")
        q_gain = sem("q_gain")
        rot_up = sem("rot_up")
        rope_ok = sem("rope_ok")
        q_ok = sem("q_ok")
        ga_silu = sem("ga_silu")
        gb_silu = sem("gb_silu")
        ua_ok = sem("ua_ok")
        tok_up = sem("tok_up")
        tok_down = sem("tok_down")
        z_up = sem("z_up")
        ya_ok = sem("ya_ok")
        yb_ok = sem("yb_ok")
        out_done = sem("out_done")

        class Attention:
            pass

        attentions = []

        def attention(name, heads, causal, q_of, k_of, v_of, pt, keys, gates, tile0, read):
            a = Attention()
            a.name, a.heads, a.causal, a.pt, a.keys, a.gates, a.tile0 = name, heads, causal, pt, keys, gates, tile0
            a.q_of, a.k_of, a.v_of = q_of, k_of, v_of
            a.n = heads * QT
            a.i0 = sum(b.n for b in attentions)
            a.p0 = sum(b.heads // 2 for b in attentions)
            a.read = read
            attentions.append(a)
            return a

        def half(h):
            return slice(HD * (h % 2), HD * (h % 2) + HD)

        def mem_attention(name, qm, kv, vm, pt, read):
            return attention(
                name, N_MEM, False,
                lambda h, qt: qm[half(h), h // 2, qt * P:(qt + 1) * P],
                lambda h, nk: kv[half(h), h // 2, 0:nk],
                lambda h, kt: vm[:, kt, h * HD:(h + 1) * HD], pt, TM, None, MT, read)

        (SP_A, SP_YA, SP_F0, SP_KV, SP_Q, SP_YF, SP_F1, SP_C0, SP_YC0, SP_C1, SP_YC1) = range(11)
        att_m0 = mem_attention("m0", qm0, mem_kv0, vm0, pt0, lambda p: (split_lo, KT * SP_YA + p + 1))
        att_f = attention(
            "fox", N_FOX, True,
            lambda h, qt: qf[half(h), h // 2, qt * P:(qt + 1) * P],
            lambda h, nk: kf[half(h), h // 2, 0:nk],
            lambda h, kt: vf[:, kt, h * HD:(h + 1) * HD], pt1, T, fl[3], 0,
            lambda p: (split_lo, KT * SP_YF + p + 1))
        att_m1 = mem_attention("m1", qm1, mem_kv1, vm1, pt1, lambda p: (split_lo, KT * SP_YF + MT + p + 1))
        att_g = [attention(
            f"gqa{l}", N_GQA, False,
            lambda h, qt: qk[half(h), h // 2, qt * P:(qt + 1) * P],
            lambda h, nk: qk[half(h), 4, 0:nk],
            lambda h, kt: vtok[:, kt, HD * (h % 2):HD * (h % 2) + HD], pt2, T, None, AT,
            lambda p, l=l: (yb_ok, AT * l + p + 1)) for l in range(2)]

        def keys_of(a, qt):
            return (qt + 1) * P if a.causal else a.keys

        NORMS = [("x", KT, D, RMS_EPS), ("mem", KT, D, RMS_EPS), ("ln", MT, MIX, LN_EPS), ("f0", KT, D, RMS_EPS),
                 ("b", KT, D, RMS_EPS), ("f1", KT, D, RMS_EPS), ("fin", KT, D, RMS_EPS)]
        for l in range(2):
            NORMS += [(f"pre{l}", KT, D, EPS_2), (f"ln{l}", AT, DA, EPS_2), (f"post{l}", KT, D, EPS_2)]
        norm_at = {}
        count = 0
        for n, (name, tiles, _, _) in enumerate(NORMS):
            norm_at[name] = (n, count)
            count += tiles
        STATS = ["x", "mem", "ln", "f0", "b", "f1", "fin", "pre0", "qk0", "ln0", "post0", "pre1", "qk1", "ln1", "post1"]
        stat_no = {name: i for i, name in enumerate(STATS)}
        cast_no = {}
        count = 0
        for name in STATS:
            cast_no[name] = count
            count += 5 if name[:2] == "qk" else 1

        X_FIN, X_C0, X_C1 = range(3)
        VT_M0, VT_F, VT_M1, VT_C0, VT_C1, VT_END = 0, 2, 2 + MT, 4 + MT, 5 + MT, 6 + MT

        block = ctx.enter_context(nc.Block())

        @block.sync
        def _(sp):
            sp.dma_start(par[:], params).then_inc(params_in, 16)
            sp.dma_start(x[:, 0:4, :], xT[:, 0:4, :]).then_inc(x_in[0], 16)
            sp.dma_start(x[:, 4:8, :], xT[:, 4:8, :]).then_inc(x_in[1], 16)
            sp.dma_start(cst[:], consts).then_inc(consts_in, 16)
            for u in range(SLOTS):
                sp.dma_start(raw[u][:], wstream[u]).then_inc(unit_in[u], 16)
                if u == 1:
                    sp.dma_start(memx[:], memT).then_inc(mem_in, 16)
            groups = UNITS // SLOTS
            with sp.Fori(1, groups) as g:
                for s in range(SLOTS):
                    sp.wait_ge(unit_lo, g * SLOTS + s - SLOTS + 1)
                    sp.dma_start(raw[s][:], wstream[g * SLOTS + s]).then_inc(unit_in[s], 16)
            for u in range(groups * SLOTS, UNITS):
                sp.wait_ge(unit_lo, u - SLOTS + 1)
                sp.dma_start(raw[u % SLOTS][:], wstream[u]).then_inc(unit_in[u % SLOTS], 16)
            for m in range(KT):
                sp.wait_ge(x_new, KT * X_C1 + m + 1)
                sp.dma_start(out[:, m, :], x[:, m, :]).then_inc(out_done, 16)
            sp.wait_ge(out_done, 16 * KT)

        @block.gpsimd
        def _(pool):
            def low(s, u):
                pool.wait_ge(unit_hi, u + 1)
                nc.gpsimd.tensor_tensor(w_lo[s][:].rearrange("p k c -> p (k c)"), raw[s][:],
                                        w_hi[s][:].rearrange("p k c -> p (k c)").bitcast(f32),
                                        SUB).then_inc(unit_lo, 1)

            def scale_probs(a):
                for i in range(a.n):
                    nk = keys_of(a, i % QT)
                    b = a.i0 + i
                    pool.wait_ge(at_inv, b + 1)
                    nc.gpsimd.tensor_scalar(prob[b % 3][:, 0:nk], prob[b % 3][:, 0:nk], rinv[:, b % 4:b % 4 + 1],
                                            1.0, MUL, MUL).then_inc(at_p, 1)

            def lows(first, end):
                n = (end - first) // SLOTS
                if n >= 2:
                    with pool.Fori(0, n) as g:
                        for j in range(SLOTS):
                            low((first + j) % SLOTS, g * SLOTS + first + j)
                    first += n * SLOTS
                for u in range(first, end):
                    low(u % SLOTS, u)

            lows(0, U_OUT0 + AHEAD)
            scale_probs(att_m0)
            lows(U_OUT0 + AHEAD, U_OUT1 + AHEAD)
            scale_probs(att_f)
            scale_probs(att_m1)
            lows(U_OUT1 + AHEAD, U_IN2 + IN2_UNITS + AHEAD)
            scale_probs(att_g[0])
            lows(U_IN2 + IN2_UNITS + AHEAD, U_IN2 + L2_UNITS + IN2_UNITS + AHEAD)
            scale_probs(att_g[1])
            lows(U_IN2 + L2_UNITS + IN2_UNITS + AHEAD, UNITS)

        @block.scalar
        def _(act):
            A = nc.scalar.activation
            own = Tally(act_did, act)

            def high(u, g=0):
                s = u % SLOTS
                if u >= SLOTS:
                    act.wait_ge(unit_used, g * SLOTS + (u - SLOTS + 1))
                act.wait_ge(unit_in[s], g * 16 + (u // SLOTS + 1) * 16)
                A(w_hi[s][:].rearrange("p k c -> p (k c)"), raw[s][:], ACT.Copy).then_inc(unit_hi, 1)

            def high_for(step):
                u = step + AHEAD
                if u < UNITS:
                    high(u)

            def split(no, gain, source, ready=None):
                for k in range(KT):
                    if ready is not None:
                        ready(k)
                    kw = {} if gain is None else {"scale": col(gain, k)}
                    A(xs_hi[:, k, :], source(k), ACT.Copy, **kw).then_inc(split_hi, 1)

            def square(name, k, source):
                base = norm_at[name][1]
                if base + k >= 2:
                    act.wait_ge(sq_added, base + k - 1)
                A(sq[(base + k) % 2][:], source, ACT.Square).then_inc(squared, 1)

            def root(name):
                n = stat_no[name]
                w = 40 if name[:2] == "qk" else 2 if name == "mem" else QT
                act.wait_ge(stat_inv, n + 1)
                if n:
                    act.wait_ge(cast_up, cast_no[name])
                A(small_r[:, 0:w], small[:, 0:w], ACT.Sqrt).then_inc(stat_root, 1)

            def residual(first, name):
                for m in range(KT):
                    high_for(first + m)
                    act.wait_ge(acc_free, accs_before(first + m) + 1)
                    square(name, m, x[:, m, :])

            def attend(a, hook):
                pairs = a.heads // 2
                for i in range(a.n + 6):
                    if i < a.n:
                        nk = keys_of(a, i % QT)
                        b = a.i0 + i
                        act.wait_ge(at_max, b + 1)
                        if b >= 3:
                            act.wait_ge(at_t, b - 2)
                        A(prob[b % 3][:, 0:nk], b_s[b % 4][:, 0:nk], ACT.Exp, bias=nmax[:, b % 4:b % 4 + 1],
                          accum_out=rsum[:, b % 4:b % 4 + 1]).then_inc(at_exp, 1)
                    if i >= 13 and (i - 13) % 8 == 0 and (i - 13) // 8 < pairs:
                        hook((i - 13) // 8)

            def out_high(a):
                def hook(p):
                    act.wait_ge(at_o, 2 * (a.p0 + p) + 2)
                    A(xs_hi[:, a.tile0 + p, :], b_o[(a.p0 + p) % 2][:], ACT.Copy).then_inc(split_hi, 1)
                return hook

            def values_down(no, dst, src_bank):
                act.wait_ge(vt_up, no + 1)
                A(dst, src_bank, ACT.Copy).then_inc(vt_down, 1)

            def ffn(l, up, dn, name):
                acc0 = accs_before(up)
                pairs0 = l * FT
                w0, b0 = PARAMS[f"w_dw_f{l}"], PARAMS[f"b_dw_f{l}"]
                with act.Fori(0, FT // 2) as g:
                    for j in range(2):
                        u = up + 2 * j
                        for e in range(2):
                            high(u + e + AHEAD, g)
                        pair = g * 2 + j
                        n = g * 2 + (pairs0 + j)
                        for e, (src, dst) in enumerate(((u_g, t_g), (u_v, t_v))):
                            act.wait_ge(acc_free, g * 4 + (acc0 + 2 * j + e + 1))
                            if e == 0:
                                act.wait_ge(h_lo, n + (l + 1))
                            ch = pair + e * FT
                            A(dst[:], src[:, 2:T + 2], ACT.Identity, scale=par[:, bass.ds(ch * 3 + (w0 + 2), 1)],
                              bias=par[:, bass.ds(ch + b0, 1)]).then_inc(tap0, 1)
                        act.wait_ge(taps, n * 2 + 1)
                        A(t_g[:], t_g[:], ACT.Silu).then_inc(silu_g, 1)
                        act.wait_ge(h_mul, n + 1)
                        A(hid_hi[:, pair, :], t_g[:], ACT.Copy).then_inc(h_hi, 1)
                for m in range(KT):
                    for c in range(DOWN_PER_TILE):
                        high_for(dn + m * DOWN_PER_TILE + c)
                    act.wait_ge(acc_free, accs_before(dn) + m + 1)
                    square(name, m, x[:, m, :])

            act.wait_ge(params_in, 16)
            for k in range(KT):
                if k % 4 == 0:
                    act.wait_ge(x_in[k // 4], 16)
                A(xs_hi[:, k, :], x[:, k, :], ACT.Copy, scale=col("g_mix0", k)).then_inc(split_hi, 1)
                square("x", k, x[:, k, :])
                if k in (1, 3, 5):
                    high(k // 2)
            act.wait_ge(consts_in, 16)
            A(ident_b[:], ident, ACT.Copy).then_inc(consts_b, 1)
            A(mask_b[:], mask, ACT.Copy).then_inc(consts_b, 1)
            root("x")
            act.wait_ge(mem_in, 16)
            for t in range(MT):
                for e in range(2):
                    high_for(2 * t + e)
                act.wait_ge(acc_free, 2 * t + 2)
                A(gate[:], gate[:], ACT.Sigmoid, bias=col("b_glu", MT + t)).then_inc(a_gate, 1)
            for u in range(U_QM0, U_MEM):
                high_for(u)
            for k in range(KT):
                A(mem_hi[:, k, :], memx[:, k, :], ACT.Copy, scale=col("g_mem", k)).then_inc(memsplit_hi, 1)
                base = norm_at["mem"][1]
                act.wait_ge(sq_added, base + k - 1)
                A(sqm[k % 2][:], memx[:, k, :], ACT.Square).then_inc(squared, 1)
            root("mem")
            for u in range(U_MEM, U_OUT0):
                high_for(u)
            for t in range(2):
                values_down(VT_M0 + t, vm0[:, :, t * P:(t + 1) * P],
                            b_vt[t][:, 0:TM].rearrange("p (k c) -> p k c", c=P))
            attend(att_m0, out_high(att_m0))
            for t in range(MT):
                act.wait_ge(s_cent, t + 1)
                square("ln", t, conv[:, t, :])
            root("ln")
            for t in range(MT):
                act.wait_ge(s_norm, t + 1)
                own.link(A(conv[:, t, :], conv[:, t, :], ACT.Silu, scale=col("ln_g", t), bias=col("ln_b", t)))
                A(xs_hi[:, t, :], conv[:, t, :], ACT.Copy).then_inc(split_hi, 1)
            residual(U_OUT0, "f0")
            split(SP_F0, "g_ffn0", lambda k: x[:, k, :])
            root("f0")
            ffn(0, U_UP0, U_DN0, "b")
            split(SP_KV, "g_kv", lambda k: x[:, k, :])
            root("b")
            for j in range(2 * MT + 1):
                high_for(U_KVF + j)
                if MT <= j - 1 < 2 * MT:
                    t = j - 1 - MT
                    values_down(VT_F + t, vf[:, :, t * P:(t + 1) * P],
                                b_vt[t % 2][:].rearrange("p (q c) -> p q c", c=P))
            act.wait_ge(unit_used, U_Q)
            split(SP_Q, "g_mix1", lambda k: x[:, k, :])
            F = slice(0, N_FOX)
            act.wait_ge(acc_free, accs_before(U_Q))
            A(fl[1][F, :], fl[0][F, :], ACT.Abs, bias=par[F, PARAMS["b_f"]:PARAMS["b_f"] + 1]).then_inc(f_act, 1)
            act.wait_ge(f_act, 1)
            A(fl[1][F, :], fl[1][F, :], ACT.Exp, scale=-1.0).then_inc(f_act, 1)
            act.wait_ge(f_act, 2)
            A(fl[1][F, :], fl[1][F, :], ACT.Ln, bias=1.0).then_inc(f_act, 1)
            for j in range(KT):
                high_for(U_Q + j)
            for t in range(2):
                values_down(VT_M1 + t, vm1[:, :, t * P:(t + 1) * P],
                            b_vt[t][:, 0:TM].rearrange("p (k c) -> p k c", c=P))
            attend(att_f, out_high(att_f))
            attend(att_m1, out_high(att_m1))
            residual(U_OUT1, "f1")
            split(SP_F1, "g_ffn1", lambda k: x[:, k, :])
            root("f1")
            ffn(1, U_UP1, U_DN1, "fin")
            root("fin")
            for l in range(2):
                u0 = U_IN2 + l * L2_UNITS
                a0 = accs_before(u0)
                for k in range(KT):
                    act.wait_ge(x_new, KT * (X_FIN if l == 0 else X_C0) + k + 1)
                    if k == 0:
                        act.dma_start(ws_sb[:], wsT[:, l]).then_inc(l2_in, 16)
                        act.dma_start(sb_sb[:], sbT[:, l]).then_inc(l2_in, 16)
                        if l == 0:
                            act.dma_start(rope_sb[:], rope).then_inc(l2_in, 16)
                    A(xs_hi[:, k, :], x[:, k, :], ACT.Copy, scale=col(f"pre_g{l}", k)).then_inc(split_hi, 1)
                    square(f"pre{l}", k, x[:, k, :])
                root(f"pre{l}")
                for j in range(IN2_UNITS):
                    high_for(u0 + j)
                    act.wait_ge(acc_free, a0 + j + 1)
                    if j < 5:
                        A(sq_qk[:, j, :], qk[:, j, :], ACT.Square).then_inc(q_sq, 1)
                        A(qk[:, j, :], qk[:, j, :], ACT.Copy,
                          scale=col(f"qn{l}" if j < 4 else f"kn{l}")).then_inc(q_gain, 1)
                    if j == 8:
                        root(f"qk{l}")
                    if j == 9:
                        values_down(VT_C0 + l, vtok[:].rearrange("p q c -> p (q c)"), b_vt[0][:])
                    if j == 11:
                        for t in range(AT):
                            act.wait_ge(s_cent, MT + AT * l + t + 1)
                            square(f"ln{l}", t, va[:, t, :])
                    if j == 13:
                        root(f"ln{l}")
                    if j == 15:
                        for t in range(AT):
                            act.wait_ge(s_norm, MT + AT * l + t + 1)
                            A(va[:, t, :], va[:, t, :], ACT.Identity, scale=col(f"lna_g{l}", t),
                              bias=col(f"lna_b{l}", t)).then_inc(s_act, 1)
                    if j in (17, 18):
                        for c in (2 * (j - 17), 2 * (j - 17) + 1):
                            act.wait_ge(tok_up, QT * l + c + 1)
                            A(va_tok[:, c, :], b_vt[c % 2][:], ACT.Copy).then_inc(tok_down, 1)
                    if 14 <= j < 18:
                        A(ga[j % 2][:], ga[j % 2][:], ACT.Silu).then_inc(ga_silu, 1)
                    if 18 <= j:
                        A(gb[:, j - 18, :], gb[:, j - 18, :], ACT.Silu).then_inc(gb_silu, 1)
                for t in range(AT):
                    act.wait_ge(ya_ok, AT * l + t + 1)
                    if t == 0:
                        act.wait_ge(unit_used, u0 + IN2_UNITS)
                    A(xs_hi[:, t, :], ua[:, t, :], ACT.Copy).then_inc(split_hi, 1)

                def gated_high(p):
                    act.wait_ge(yb_ok, AT * l + p + 1)
                    A(xs_hi[:, AT + p, :], gb[:, p, :], ACT.Copy).then_inc(split_hi, 1)

                attend(att_g[l], gated_high)
                for m in range(KT):
                    high_for(u0 + IN2_UNITS + m)
                    act.wait_ge(acc_free, a0 + IN2_UNITS + m + 1)
                    square(f"post{l}", m, o_sb(m))
                root(f"post{l}")

        @block.vector
        def _(dve):
            V = nc.vector
            own = Tally(dve_did, dve)

            def take_acc(u, a):
                dve.wait_ge(unit_used, u + 1)
                return acc[a % 2]

            def scaled(dst, u, width=T, by=None, factor=None):
                src = take_acc(u, accs_before(u))
                by = rstd if by is None else by
                p = dst.shape[0]
                if factor is None:
                    V.tensor_tensor(dst, src[0:p, 0:width], by[0:p, 0:width], MUL).then_inc(acc_free, 1)
                else:
                    V.scalar_tensor_tensor(out=dst, in0=src[0:p, 0:width], scalar=factor, in1=by[0:p, 0:width],
                                           op0=MUL, op1=MUL).then_inc(acc_free, 1)

            def split(no, gain, source, ready=None):
                for k in range(KT):
                    dve.wait_ge(split_hi, KT * no + k + 1)
                    kw = 1.0 if gain is None else col(gain, k)
                    V.scalar_tensor_tensor(out=xs_lo[:, k, :], in0=source(k), scalar=kw,
                                           in1=xs_hi[:, k, :].bitcast(f32), op0=MUL, op1=SUB).then_inc(split_lo, 1)

            def add_square(name, k, first_waits=True):
                base = norm_at[name][1]
                dve.wait_ge(squared, base + k + 1)
                src = sq[(base + k) % 2][:]
                if k == 0:
                    V.tensor_copy(sq_sum[:], src).then_inc(sq_added, 1)
                else:
                    dve.wait_ge(sq_added, base + k)
                    V.tensor_tensor(sq_sum[:], sq_sum[:], src, ADD).then_inc(sq_added, 1)

            def invert(name):
                n = stat_no[name]
                if name[:2] == "qk":
                    w, channels, eps = 40, HD, EPS_2
                else:
                    w = QT
                    _, _, channels, eps = NORMS[norm_at[name][0]]
                if name == "mem":
                    w = 2
                dve.wait_ge(stat_up, n + 1)
                if n >= 1:
                    dve.wait_ge(stat_root, n)
                own.link(V.tensor_scalar(small[:, 0:w], b_stat[:, 0:w], 1.0 / channels, eps, MUL, ADD))
                V.reciprocal(small[:, 0:w], small[:, 0:w]).then_inc(stat_inv, 1)

            def spread(name, dst, width=T):
                dve.wait_ge(cast_up, cast_no[name] + 1)
                V.tensor_copy(dst[:, 0:width], b_cast[:, 0:width]).then_inc(cast_down, 1)
                dve.wait_ge(cast_down, cast_no[name] + 1)

            def residual(first, name):
                for m in range(KT):
                    u = first + m
                    src = take_acc(u, accs_before(u))
                    V.tensor_tensor(x[:, m, :], x[:, m, :], src[:], ADD).then_inc(acc_free, 1)
                    add_square(name, m)

            def attend(a, hook):
                pairs = a.heads // 2
                for i in range(a.n + 6):
                    if i < a.n:
                        nk = keys_of(a, i % QT)
                        b = a.i0 + i
                        dve.wait_ge(at_s, b + 1)
                        if b >= 4:
                            dve.wait_ge(at_exp, b - 3)
                        V.tensor_reduce(nmax[:, b % 4:b % 4 + 1], b_s[b % 4][:, 0:nk], AX.X, ALU.max,
                                        negate=True).then_inc(at_max, 1)
                    if 1 <= i <= a.n:
                        b = a.i0 + i - 1
                        dve.wait_ge(at_exp, b + 1)
                        if b >= 4:
                            dve.wait_ge(at_p, b - 3)
                        V.reciprocal(rinv[:, b % 4:b % 4 + 1], rsum[:, b % 4:b % 4 + 1]).then_inc(at_inv, 1)
                    if 2 <= i <= a.n + 1:
                        j = i - 2
                        h, qt = j // QT, j % QT
                        nt = keys_of(a, qt) // P
                        b = a.i0 + j
                        dve.wait_ge(at_t, b + 1)
                        if qt == 0 and h >= 2:
                            dve.wait_ge(at_o, 2 * a.p0 + h - 1)
                        V.tensor_copy(a.pt[h % 2][:, 0:nt, qt * P:(qt + 1) * P],
                                      b_t[b % 2][:, 0:nt * P].rearrange("p (k q) -> p k q", q=P)).then_inc(at_pt, 1)
                    if i >= 13 and (i - 13) % 8 == 0 and (i - 13) // 8 < pairs:
                        hook((i - 13) // 8)

            def out_low(a, no):
                def hook(p):
                    k = a.tile0 + p
                    first = p if a.tile0 == 0 or no == SP_YA else a.tile0 + p
                    dve.wait_ge(split_hi, KT * no + first + 1)
                    V.tensor_tensor(xs_lo[:, k, :], b_o[(a.p0 + p) % 2][:], xs_hi[:, k, :].bitcast(f32),
                                    SUB).then_inc(split_lo, 1)
                return hook

            def ffn(l, up, dn, name):
                acc0 = accs_before(up)
                pairs0 = l * FT
                w0 = PARAMS[f"w_dw_f{l}"]
                own.link(V.memset(u_g[:, 0:2], 0.0))
                V.memset(u_v[:, 0:2], 0.0).then_inc(h_lo, 1)
                dve.wait_ge(h_lo, pairs0 + l + 1)
                with dve.Fori(0, FT // 2) as g:
                    for j in range(2):
                        pair = g * 2 + j
                        n = g * 2 + (pairs0 + j)
                        for e, dst in enumerate((u_g, u_v)):
                            dve.wait_ge(unit_used, g * 4 + (up + 2 * j + e + 1))
                            V.tensor_tensor(dst[:, 2:T + 2], acc[(acc0 + e) % 2][:], rstd[:], MUL).then_inc(acc_free, 1)
                        for e, (src, dst) in enumerate(((u_g, t_g), (u_v, t_v))):
                            ch = pair + e * FT
                            dve.wait_ge(tap0, n * 2 + (e + 1))
                            V.scalar_tensor_tensor(out=dst[:], in0=src[:, 1:1 + T],
                                                   scalar=par[:, bass.ds(ch * 3 + (w0 + 1), 1)], in1=dst[:],
                                                   op0=MUL, op1=ADD).then_inc(tap_mid, 1)
                            dve.wait_ge(tap_mid, n * 2 + (e + 1))
                            V.scalar_tensor_tensor(out=dst[:], in0=src[:, 0:T],
                                                   scalar=par[:, bass.ds(ch * 3 + w0, 1)], in1=dst[:],
                                                   op0=MUL, op1=ADD).then_inc(taps, 1)
                        dve.wait_ge(taps, n * 2 + 2)
                        dve.wait_ge(silu_g, n + 1)
                        V.tensor_tensor(t_g[:], t_g[:], t_v[:], MUL).then_inc(h_mul, 1)
                        dve.wait_ge(h_hi, n + 1)
                        V.tensor_tensor(hid_lo[:, pair, :], t_g[:], hid_hi[:, pair, :].bitcast(f32),
                                        SUB).then_inc(h_lo, 1)
                for m in range(KT):
                    dve.wait_ge(unit_used, dn + (m + 1) * DOWN_PER_TILE)
                    V.tensor_tensor(x[:, m, :], x[:, m, :], acc[(accs_before(dn) + m) % 2][:],
                                    ADD).then_inc(acc_free, 1)
                    add_square(name, m)

            dve.wait_ge(params_in, 16)
            dve.wait_ge(x_in[0], 16)
            dve.wait_ge(x_in[1], 16)
            for t in range(MT):
                V.memset(glu[:, t, 0:CW - 1], 0.0).then_inc(dve_did, 1)
                own.n += 1
            for k in range(KT):
                dve.wait_ge(split_hi, KT * SP_A + k + 1)
                V.scalar_tensor_tensor(out=xs_lo[:, k, :], in0=x[:, k, :], scalar=col("g_mix0", k),
                                       in1=xs_hi[:, k, :].bitcast(f32), op0=MUL, op1=SUB).then_inc(split_lo, 1)
                add_square("x", k)
            invert("x")
            spread("x", rstd)
            own.wait()
            for t in range(MT):
                u = U_GLU + 2 * t
                scaled(glu[:, t, CW - 1:], u)
                scaled(gate[:], u + 1)
                dve.wait_ge(a_gate, t + 1)
                own.link(V.scalar_tensor_tensor(out=glu[:, t, CW - 1:], in0=glu[:, t, CW - 1:],
                                                scalar=col("b_glu", t), in1=gate[:], op0=ADD, op1=MUL))
                own.link(V.tensor_scalar(conv[:, t, :], glu[:, t, 0:T], col("w_dw_a", t * CW), col("b_dw_a", t),
                                         MUL, ADD))
                for tap in range(1, CW):
                    own.link(V.scalar_tensor_tensor(out=conv[:, t, :], in0=glu[:, t, tap:tap + T],
                                                    scalar=col("w_dw_a", t * CW + tap), in1=conv[:, t, :],
                                                    op0=MUL, op1=ADD))
            for j in range(2):
                scaled(qm0[:, j, :], U_QM0 + j, factor=HD ** -0.5)
            for k in range(KT):
                dve.wait_ge(memsplit_hi, k + 1)
                V.scalar_tensor_tensor(out=mem_lo[:, k, :], in0=memx[:, k, :], scalar=col("g_mem", k),
                                       in1=mem_hi[:, k, :].bitcast(f32), op0=MUL, op1=SUB).then_inc(memsplit_lo, 1)
                base = norm_at["mem"][1]
                dve.wait_ge(squared, base + k + 1)
                if k == 0:
                    V.tensor_copy(sqm_sum[:], sqm[k % 2][:]).then_inc(sq_added, 1)
                else:
                    dve.wait_ge(sq_added, base + k)
                    V.tensor_tensor(sqm_sum[:], sqm_sum[:], sqm[k % 2][:], ADD).then_inc(sq_added, 1)
            invert("mem")
            spread("mem", rstd_m, TM)
            for j in range(8):
                dst = mem_kv0 if j < 4 else mem_kv1
                scaled(dst[:, j % 4, :], U_MEM + j, TM, rstd_m)
            attend(att_m0, out_low(att_m0, SP_YA))

            def layer_norm(name, base, src, n):
                dve.wait_ge(sum_up, base[0] + 1)
                for t in range(n):
                    V.scalar_tensor_tensor(out=src[:, t, :], in0=b_vt[1][:], scalar=-1.0 / (n * P), in1=src[:, t, :],
                                           op0=MUL, op1=ADD).then_inc(s_cent, 1)

            def partial_sum(src, n, last):
                own.link(V.tensor_tensor(chan_sum[:], src[:, 0, :], src[:, 1, :], ADD))
                for t in range(2, n):
                    if t < n - 1:
                        own.link(V.tensor_tensor(chan_sum[:], chan_sum[:], src[:, t, :], ADD))
                    else:
                        V.tensor_tensor(chan_sum[:], chan_sum[:], src[:, t, :], ADD).then_inc(s_sum, 1)

            partial_sum(conv, MT, None)
            layer_norm("ln", (0,), conv, MT)
            for t in range(MT):
                add_square("ln", t)
            invert("ln")
            spread("ln", rstd_ln)
            for t in range(MT):
                V.tensor_tensor(conv[:, t, :], conv[:, t, :], rstd_ln[:], MUL).then_inc(s_norm, 1)
            for t in range(MT):
                dve.wait_ge(split_hi, KT * SP_YA + 2 + t + 1)
                V.tensor_tensor(xs_lo[:, t, :], conv[:, t, :], xs_hi[:, t, :].bitcast(f32), SUB).then_inc(split_lo, 1)
            residual(U_OUT0, "f0")
            split(SP_F0, "g_ffn0", lambda k: x[:, k, :])
            invert("f0")
            spread("f0", rstd)
            ffn(0, U_UP0, U_DN0, "b")
            split(SP_KV, "g_kv", lambda k: x[:, k, :])
            invert("b")
            spread("b", rstd)
            for t in range(MT):
                scaled(kf[:, t, :], U_KVF + t)
            for t in range(MT):
                if t >= 2:
                    dve.wait_ge(vt_up, VT_F + t - 1)
                scaled(vst[t % 2][:], U_KVF + MT + t)
            F = slice(0, N_FOX)
            scaled(fl[0][F, :], U_KVF + 2 * MT)
            dve.wait_ge(acc_free, accs_before(U_Q))
            own.link(V.tensor_scalar(fl[2][F, :], fl[0][F, :], par[F, PARAMS["b_f"]:PARAMS["b_f"] + 1], 0.0,
                                     ADD, ALU.min))
            split(SP_Q, "g_mix1", lambda k: x[:, k, :])
            dve.wait_ge(f_act, 3)
            own.link(V.tensor_tensor(fl[0][F, :], fl[1][F, :], fl[2][F, :], SUB))
            own.link(V.memset(fl[2][F, :], 1.0))
            V.tensor_tensor_scan(fl[3][F, :], fl[2][F, :], fl[0][F, :], 0.0, MUL, ADD).then_inc(f_done, 1)
            for t in range(MT):
                scaled(qf[:, t, :], U_Q + t, factor=HD ** -0.5)
            for t in range(2):
                scaled(qm1[:, t, :], U_Q + MT + t, factor=HD ** -0.5)
            attend(att_f, out_low(att_f, SP_YF))
            attend(att_m1, out_low(att_m1, SP_YF))
            residual(U_OUT1, "f1")
            split(SP_F1, "g_ffn1", lambda k: x[:, k, :])
            invert("f1")
            spread("f1", rstd)
            ffn(1, U_UP1, U_DN1, "fin")
            invert("fin")
            spread("fin", rstd)

            def enter(l, update):
                for k in range(KT + 1):
                    if k < KT:
                        update(k)
                    if k > 0 and l < 2:
                        j = k - 1
                        dve.wait_ge(split_hi, KT * (SP_C0, SP_C1)[l] + j + 1)
                        V.scalar_tensor_tensor(out=xs_lo[:, j, :], in0=x[:, j, :], scalar=col(f"pre_g{l}", j),
                                               in1=xs_hi[:, j, :].bitcast(f32), op0=MUL, op1=SUB).then_inc(split_lo, 1)
                        add_square(f"pre{l}", j)

            def final_norm(k):
                V.scalar_tensor_tensor(out=x[:, k, :], in0=x[:, k, :], scalar=col("g_final", k), in1=rstd[:],
                                       op0=MUL, op1=MUL).then_inc(x_new, 1)

            enter(0, final_norm)
            for l in range(2):
                u0 = U_IN2 + l * L2_UNITS
                a0 = accs_before(u0)
                invert(f"pre{l}")
                spread(f"pre{l}", rstd)
                dve.wait_ge(l2_in, 48 + 32 * l)
                for j in range(IN2_UNITS):
                    dst = (qk[:, j, :] if j < 5 else vch[:] if j == 5 else va[:, j - 6, :] if j < 10
                           else ua[:, j - 10, :] if j < 14 else ga[j % 2][:] if j < 18 else gb[:, j - 18, :])
                    scaled(dst, u0 + j)
                    if 6 <= j < 11:
                        t = j - 6
                        dve.wait_ge(q_gain, 5 * l + t + 1)
                        dve.wait_ge(rot_up, 5 * l + t + 1)
                        own.link(V.tensor_tensor(roped[:], b_s[2 + t % 2][:], rope_sb[:, 1, :], MUL))
                        own.link(V.tensor_tensor(qk[:, t, :], qk[:, t, :], rope_sb[:, 0, :], MUL))
                        V.tensor_tensor(qk[:, t, :], qk[:, t, :], roped[:], ADD).then_inc(rope_ok, 1)
                        dve.wait_ge(rope_ok, 5 * l + t + 1)
                    if j == 7:
                        invert(f"qk{l}")
                    if j == 9:
                        dve.wait_ge(acc_free, a0 + 10)
                        partial_sum(va, AT, None)
                    if 9 <= j < 14:
                        t = j - 9
                        dve.wait_ge(cast_up, cast_no[f"qk{l}"] + t + 1)
                        V.scalar_tensor_tensor(out=qk[:, t, :], in0=qk[:, t, :], scalar=HD ** -0.5 if t < 4 else 1.0,
                                               in1=b_cast[:], op0=MUL, op1=MUL).then_inc(cast_down, 1)
                    if j == 10:
                        layer_norm(f"ln{l}", (1 + l,), va, AT)
                    if j == 11:
                        for t in range(AT):
                            add_square(f"ln{l}", t)
                    if j == 12:
                        invert(f"ln{l}")
                    if j == 14:
                        spread(f"ln{l}", rstd_ln)
                        for t in range(AT):
                            V.tensor_tensor(va[:, t, :], va[:, t, :], rstd_ln[:], MUL).then_inc(s_norm, 1)
                    if 15 <= j < 19:
                        t = j - 15
                        dve.wait_ge(ga_silu, AT * l + t + 1)
                        own.link(V.tensor_tensor(ua[:, t, :], ua[:, t, :], ga[(14 + t) % 2][:], MUL))
                    if j >= 18:
                        t = j - 18
                        dve.wait_ge(z_up, AT * l + t + 1)
                        own.link(V.tensor_tensor(va[:, t, :].rearrange("p (c i) -> p c i", i=P),
                                                 b_s[2 + t % 2][:].rearrange("p (c i) -> p c i", i=P),
                                                 sb_sb[:, t:t + 1, :].to_broadcast([P, QT, P]), ADD))
                        V.tensor_tensor(ua[:, t, :], ua[:, t, :], va[:, t, :], MUL).then_inc(ya_ok, 1)
                no = (SP_YC0, SP_YC1)[l]
                for t in range(AT):
                    dve.wait_ge(split_hi, KT * no + t + 1)
                    V.tensor_tensor(xs_lo[:, t, :], ua[:, t, :], xs_hi[:, t, :].bitcast(f32), SUB).then_inc(split_lo, 1)

                def low(p):
                    dve.wait_ge(split_hi, KT * no + AT + p + 1)
                    V.tensor_tensor(xs_lo[:, AT + p, :], gb[:, p, :], xs_hi[:, AT + p, :].bitcast(f32),
                                    SUB).then_inc(split_lo, 1)

                def gated(p):
                    dve.wait_ge(at_o, 2 * (att_g[l].p0 + p) + 2)
                    dve.wait_ge(gb_silu, AT * l + p + 1)
                    V.tensor_tensor(gb[:, p, :], b_o[(att_g[l].p0 + p) % 2][:], gb[:, p, :], MUL).then_inc(yb_ok, 1)
                    if p:
                        low(p - 1)

                attend(att_g[l], gated)
                low(AT - 1)
                for m in range(KT):
                    u = u0 + IN2_UNITS + m
                    src = take_acc(u, accs_before(u))
                    V.tensor_copy(o_sb(m), src[:]).then_inc(acc_free, 1)
                    add_square(f"post{l}", m)
                invert(f"post{l}")
                spread(f"post{l}", rstd)

                def post(k):
                    own.link(V.scalar_tensor_tensor(out=o_sb(k), in0=o_sb(k), scalar=col(f"post_g{l}", k), in1=rstd[:],
                                                    op0=MUL, op1=MUL))
                    V.tensor_tensor(x[:, k, :], x[:, k, :], o_sb(k), ADD).then_inc(x_new, 1)

                enter(l + 1, post)

        @block.tensor
        def _(pe):
            MM = nc.tensor.matmul

            def products(dst, slot, k, hi, lo, start, stop):
                MM(dst, w_hi[slot][:, k, :], hi, start=start, stop=False)
                MM(dst, w_hi[slot][:, k, :], lo, start=False, stop=False)
                return MM(dst, w_lo[slot][:, k, :], hi, start=False, stop=stop)

            def unit(u, a, hi=xs_hi, lo=xs_lo, width=T, first=None, hook=None, g=0, first_sem=None):
                slot = u % SLOTS
                pe.wait_ge(unit_lo, g * SLOTS + (u + 1))
                if a >= 2:
                    pe.wait_ge(acc_free, g * SLOTS + (a - 1))
                for k in range(KT):
                    if first is not None:
                        pe.wait_ge(split_lo if first_sem is None else first_sem, first + k + 1)
                    last = products(acc[a % 2][:, 0:width], slot, k, hi[:, k, :], lo[:, k, :], k == 0, k == KT - 1)
                    if k == 3 and hook is not None:
                        hook()
                last.then_inc(unit_used, 1)

            def stat(name, src=sq_sum, tiles=QT):
                _, base = norm_at[name]
                count = NORMS[norm_at[name][0]][1]
                pe.wait_ge(sq_added, base + count)
                n = stat_no[name]
                if n:
                    pe.wait_ge(stat_inv, n)
                for q in range(tiles):
                    last = MM(b_stat[:, q:q + 1], src[:, q * P:(q + 1) * P], ones[:, 0:1], start=True, stop=True)
                last.then_inc(stat_up, 1)

            def cast(name, tiles=QT):
                c = cast_no[name]
                pe.wait_ge(stat_root, stat_no[name] + 1)
                if c:
                    pe.wait_ge(cast_down, c)
                for q in range(tiles):
                    last = MM(b_cast[:, q * P:(q + 1) * P], small_r[:, q:q + 1].to_broadcast([P, P]), ident,
                              start=True, stop=True)
                last.then_inc(cast_up, 1)

            def values_up(no, src, parts):
                if no >= 2:
                    pe.wait_ge(vt_down, no - 1)
                b = b_vt[0 if no >= VT_C0 else no % 2 if no < VT_F else (no - VT_F) % 2]
                for q in range(parts):
                    last = nc.tensor.transpose(b[:, q * P:(q + 1) * P], src[:, q * P:(q + 1) * P], ident)
                last.then_inc(vt_up, 1)

            def attend(a):
                def scores(i):
                    b = a.i0 + i
                    h, qt = i // QT, i % QT
                    nk = keys_of(a, qt)
                    if b >= 4:
                        pe.wait_ge(at_exp, b - 3)
                    dst = b_s[b % 4][:, 0:nk]
                    last = MM(dst, a.q_of(h, qt), a.k_of(h, nk), start=True, stop=not a.causal)
                    if a.causal:
                        MM(dst, ident[0:N_FOX, h:h + 1].to_broadcast([N_FOX, P]), a.gates[0:N_FOX, 0:nk],
                           start=False, stop=False)
                        last = MM(b_s[b % 4][:, nk - P:nk], ident_b[:], mask_b[:], start=False, stop=True)
                    last.then_inc(at_s, 1)

                def transposes(i):
                    b = a.i0 + i
                    pe.wait_ge(at_p, b + 1)
                    if b >= 2:
                        pe.wait_ge(at_pt, b - 1)
                    for k in range(keys_of(a, i % QT) // P):
                        last = nc.tensor.transpose(b_t[b % 2][:, k * P:(k + 1) * P],
                                                   prob[b % 3][:, k * P:(k + 1) * P], ident)
                    last.then_inc(at_t, 1)

                def output(h):
                    p = a.p0 + h // 2
                    pe.wait_ge(at_pt, a.i0 + QT * (h + 1))
                    if h % 2 == 0 and p >= 2:
                        pair = p - 2
                        b = [c for c in attentions if c.p0 <= pair][-1]
                        s, v = b.read(pair - b.p0)
                        pe.wait_ge(s, v)
                    nt = a.keys // P
                    for k in range(nt):
                        q0 = k * P if a.causal else 0
                        last = MM(b_o[p % 2][half(h), q0:T], a.v_of(h, k), a.pt[h % 2][:, k, q0:T],
                                  start=(k == 0), stop=(k == nt - 1))
                    last.then_inc(at_o, 1)

                for i in range(3):
                    scores(i)
                for i in range(a.n):
                    transposes(i)
                    if i + 3 < a.n:
                        scores(i + 3)
                    if i % QT == 1 and i > QT:
                        output(i // QT - 1)
                output(a.heads - 1)

            def ffn(l, up, dn, name, no):
                a0 = accs_before(up)
                for j in range(4):
                    hook = None
                    if j == 0:
                        hook = lambda: stat(name)
                    if j == 1:
                        hook = lambda: cast(name)
                    unit(up + j, a0 + j, first=KT * no if j == 0 else None, hook=hook)
                with pe.Fori(1, UP_UNITS // 4) as g:
                    for j in range(4):
                        unit(up + j, a0 + j, g=g)
                a0 = accs_before(dn)
                pe.wait_ge(h_lo, (l + 1) * (FT + 1))
                with pe.Fori(0, 2) as g:
                    for m in range(4):
                        pe.wait_ge(acc_free, g * 4 + (a0 + m - 1))
                        for c in range(DOWN_PER_TILE):
                            u = dn + m * DOWN_PER_TILE + c
                            pe.wait_ge(unit_lo, g * (4 * DOWN_PER_TILE) + (u + 1))
                            for k in range(KT):
                                t = c * KT + k
                                if t < FT:
                                    last = products(acc[(a0 + m) % 2][:], u % SLOTS, k, hid_hi[:, t, :],
                                                    hid_lo[:, t, :], t == 0, t == FT - 1)
                            last.then_inc(unit_used, 1)

            pe.wait_ge(consts_in, 16)
            for j in range(2 * MT + 2):
                unit(j, j, first=KT * SP_A if j == 0 else None,
                     hook=(lambda: stat("x")) if j == 0 else (lambda: cast("x")) if j == 1 else None)
            stat("mem", sqm_sum, 2)
            for j in range(8):
                unit(U_MEM + j, accs_before(U_MEM + j), mem_hi, mem_lo, TM, first=0 if j == 0 else None,
                     hook=(lambda: cast("mem", 2)) if j == 0 else None, first_sem=memsplit_lo)
            pe.wait_ge(acc_free, accs_before(U_OUT0))
            for t in range(2):
                values_up(VT_M0 + t, mem_kv0[:, 2 + t, :], 2)
            pe.wait_ge(vt_down, VT_M0 + 2)
            attend(att_m0)
            pe.wait_ge(s_sum, 1)
            pe.wait_ge(at_pt, att_m0.i0 + att_m0.n)
            MM(b_vt[1][:], ones, chan_sum[:], start=True, stop=True).then_inc(sum_up, 1)
            stat("ln")
            cast("ln")
            pe.wait_ge(at_exp, att_m0.i0 + att_m0.n)
            pe.wait_ge(split_lo, KT * (SP_YA + 1))
            for m in range(KT):
                unit(U_OUT0 + m, accs_before(U_OUT0 + m))
            ffn(0, U_UP0, U_DN0, "f0", SP_F0)
            for j in range(2 * MT + 1):
                unit(U_KVF + j, accs_before(U_KVF + j), first=KT * SP_KV if j == 0 else None,
                     hook=(lambda: stat("b")) if j == 0 else (lambda: cast("b")) if j == 1 else None)
                if j > MT:
                    t = j - 1 - MT
                    pe.wait_ge(acc_free, accs_before(U_KVF + MT + t) + 1)
                    values_up(VT_F + t, vst[t % 2], QT)
            for j in range(KT):
                unit(U_Q + j, accs_before(U_Q + j), first=KT * SP_Q if j == 0 else None)
            pe.wait_ge(acc_free, accs_before(U_OUT1))
            pe.wait_ge(vt_down, VT_M1)
            for t in range(2):
                values_up(VT_M1 + t, mem_kv1[:, 2 + t, :], 2)
            pe.wait_ge(vt_down, VT_M1 + 2)
            pe.wait_ge(f_done, 1)
            pe.wait_ge(consts_b, 2)
            attend(att_f)
            attend(att_m1)
            pe.wait_ge(at_exp, att_m1.i0 + att_m1.n)
            pe.wait_ge(split_lo, KT * (SP_YF + 1))
            for m in range(KT):
                unit(U_OUT1 + m, accs_before(U_OUT1 + m))
            ffn(1, U_UP1, U_DN1, "f1", SP_F1)
            stat("fin")
            cast("fin")
            for l in range(2):
                u0 = U_IN2 + l * L2_UNITS
                a0 = accs_before(u0)
                for j in range(IN2_UNITS):
                    unit(u0 + j, a0 + j, first=KT * (SP_C0, SP_C1)[l] if j == 0 else None,
                         hook=(lambda: stat(f"pre{l}")) if j == 0 else (lambda: cast(f"pre{l}")) if j == 1 else None)
                    if 6 <= j < 11:
                        t = j - 6
                        pe.wait_ge(q_gain, 5 * l + t + 1)
                        if t >= 2:
                            pe.wait_ge(rope_ok, 5 * l + t - 1)
                        MM(b_s[2 + t % 2][:], rotm, qk[:, t, :], start=True, stop=True).then_inc(rot_up, 1)
                    if j == 7:
                        n = stat_no[f"qk{l}"]
                        pe.wait_ge(q_sq, 5 * (l + 1))
                        pe.wait_ge(stat_inv, n)
                        for t in range(5):
                            for q in range(QT):
                                c = 2 * (t * QT + q)
                                last = MM(b_stat[:, c:c + 2], sq_qk[:, t, q * P:(q + 1) * P], headsel,
                                          start=True, stop=True)
                        last.then_inc(stat_up, 1)
                    if j == 8:
                        pe.wait_ge(acc_free, a0 + 6)
                        values_up(VT_C0 + l, vch, QT)
                    if 9 <= j < 14:
                        t = j - 9
                        pe.wait_ge(stat_root, stat_no[f"qk{l}"] + 1)
                        pe.wait_ge(cast_down, cast_no[f"qk{l}"] + t)
                        for q in range(QT):
                            for h in range(2):
                                c = 2 * (t * QT + q) + h
                                last = MM(b_cast[HD * h:HD * (h + 1), q * P:(q + 1) * P],
                                          small_r[:, c:c + 1].to_broadcast([P, HD]), ident, start=True, stop=True)
                        last.then_inc(cast_up, 1)
                    if j == 10:
                        pe.wait_ge(s_sum, 2 + l)
                        MM(b_vt[1][:], ones, chan_sum[:], start=True, stop=True).then_inc(sum_up, 1)
                    if j == 12:
                        stat(f"ln{l}")
                    if j == 14:
                        cast(f"ln{l}")
                    if j in (16, 17):
                        pe.wait_ge(s_act, AT * (l + 1))
                        pe.wait_ge(vt_down, VT_C0 + l + 1)
                        for c in (2 * (j - 16), 2 * (j - 16) + 1):
                            n = QT * l + c
                            if n >= 2:
                                pe.wait_ge(tok_down, n - 1)
                            for t in range(AT):
                                last = nc.tensor.transpose(b_vt[c % 2][:, t * P:(t + 1) * P],
                                                           va[:, t, c * P:(c + 1) * P], ident)
                            last.then_inc(tok_up, 1)
                    if j >= 18:
                        t = j - 18
                        pe.wait_ge(l2_in, 48 + 32 * l)
                        pe.wait_ge(tok_down, QT * (l + 1))
                        pe.wait_ge(rope_ok, 5 * (l + 1))
                        if t >= 2:
                            pe.wait_ge(ya_ok, AT * l + t - 1)
                        for c in range(QT):
                            for h in range(2):
                                last = MM(b_s[2 + t % 2][HD * h:HD * (h + 1), c * P:(c + 1) * P],
                                          va_tok[:, c, t * P + HD * h:t * P + HD * (h + 1)], ws_sb[:, 2 * t + h, :],
                                          start=True, stop=True)
                        last.then_inc(z_up, 1)
                pe.wait_ge(acc_free, a0 + IN2_UNITS)
                pe.wait_ge(cast_down, cast_no[f"ln{l}"] + 1)
                pe.wait_ge(ya_ok, AT * (l + 1))
                attend(att_g[l])
                pe.wait_ge(at_exp, att_g[l].i0 + att_g[l].n)
                pe.wait_ge(split_lo, KT * ((SP_YC0, SP_YC1)[l] + 1))
                for m in range(KT):
                    unit(u0 + IN2_UNITS + m, a0 + IN2_UNITS + m)
                stat(f"post{l}")
                cast(f"post{l}")


def _tiles(w):
    import numpy as np
    rows, cols = w.shape
    pad = -rows % (KT * P)
    w = np.concatenate([w, np.zeros((pad, cols), w.dtype)]) if pad else w
    w = w.reshape(-1, KT, P, cols // P, P)
    return np.ascontiguousarray(w.transpose(3, 0, 2, 1, 4)).reshape(-1, P, UNIT)


def _pairs(w, first, second):
    import numpy as np
    a, b = _tiles(w[:, first]), _tiles(w[:, second])
    return np.stack([a, b], 1).reshape(-1, P, UNIT)


def _heads_by_pair(n_groups_first):
    return [c for t in range(4) for h in (t, t + 4) for c in range(h * HD, (h + 1) * HD)]


def _stream(a):
    import numpy as np
    w_in = a["w_in_a"][0]
    kvf = a["w_kvf"]
    f = np.concatenate([kvf[:, 2 * MIX:], np.zeros((D, P - N_FOX), kvf.dtype)], 1)
    order = _heads_by_pair(4)
    parts = [_pairs(w_in, slice(0, MIX), slice(MIX, 2 * MIX)), _tiles(w_in[:, 2 * MIX:]),
             _tiles(a["w_mem_kv"][0]), _tiles(a["w_mem_kv"][1]), _tiles(a["w_out"][0])]
    for l in range(2):
        if l == 1:
            parts += [_tiles(kvf[:, :2 * MIX]), _tiles(f), _tiles(a["w_in_b"][0]), _tiles(a["w_out"][1])]
        up = a["w_up"][l]
        parts += [_pairs(up, slice(0, DFF), slice(DFF, 2 * DFF)), _tiles(a["w_down"][l])]
    for l in range(2):
        w = a["w_in_2"][l]
        u, v, g, q, k, vv, gb = np.split(w, np.cumsum([DA, DA, DA, DA, P, P]), axis=1)
        parts += [_tiles(m) for m in (q[:, order], k, vv, v, u, g, gb[:, order])]
        w = a["w_out_2"][l]
        parts.append(_tiles(np.concatenate([w[:DA], w[DA:][order]])))
    return np.concatenate(parts)


def _params(a):
    import numpy as np
    cols = np.zeros((P, N_PARAMS), np.float32)

    def put(name, v):
        v = np.asarray(v)
        if v.ndim == 1:
            v = v[:, None]
        n = v.shape[0] // P
        v = v.reshape(n, P, -1).transpose(1, 0, 2).reshape(P, -1)
        cols[:, PARAMS[name]:PARAMS[name] + v.shape[1]] = v

    for l in range(2):
        put(f"g_mix{l}", a["g_mix"][l])
        put(f"g_ffn{l}", a["g_ffn"][l])
        put(f"w_dw_f{l}", a["w_dw_f"][l].T)
        put(f"b_dw_f{l}", a["b_dw_f"][l])
        put(f"pre_g{l}", a["pre_g_2"][l])
        put(f"post_g{l}", a["post_g_2"][l])
        put(f"lna_g{l}", a["ln_a_g_2"][l])
        put(f"lna_b{l}", a["ln_a_b_2"][l])
        put(f"qn{l}", np.tile(a["q_norm_g_2"][l], 2))
        put(f"kn{l}", np.tile(a["k_norm_g_2"][l], 2))
    put("b_glu", a["b_glu"][0])
    put("w_dw_a", a["w_dw_a"][0].T)
    put("b_dw_a", a["b_dw_a"][0])
    put("ln_g", a["ln_g"][0])
    put("ln_b", a["ln_b"][0])
    put("g_kv", a["g_kv"])
    put("g_mem", a["g_mem"])
    put("g_final", a["g_final"])
    put("b_f", np.concatenate([a["b_f"], np.zeros(P - N_FOX, np.float32)]))
    return cols


def _consts():
    import numpy as np
    c = np.zeros((P, 4 * P + 2), np.float32)
    c[:, 0:P] = np.eye(P)
    c[:, P:2 * P] = 1.0
    for m in range(P):
        if m % 32 < 16:
            c[m + 16, 2 * P + m] = -1.0
        else:
            c[m - 16, 2 * P + m] = 1.0
    q, k = np.arange(P)[:, None], np.arange(P)[None, :]
    c[:, 3 * P:4 * P] = np.where(k > q, np.float32(NEG), np.float32(0.0))
    c[0:HD, 4 * P] = 1.0
    c[HD:P, 4 * P + 1] = 1.0
    return c


def _rope():
    import numpy as np
    inv = np.float32(10000.0) ** (-np.arange(0, 32, 2, dtype=np.float32) / np.float32(32))
    t = np.arange(T)
    pos = [(t // 64).astype(np.float32), (t % 64).astype(np.float32)]
    ang = np.stack([pos[(p % HD) // 32] * inv[p % 16] for p in range(P)])
    return np.stack([np.cos(ang), np.sin(ang)], 1).astype(np.float32)


def kernel(**inputs):
    import numpy as np
    import concourse.bacc as bacc
    from concourse.bass_utils import run_bass_kernel_spmd

    a = {k: np.asarray(v) for k, v in inputs.items()}
    by_channel = lambda v, n: np.ascontiguousarray(v.reshape(n, KT, P).transpose(2, 1, 0))
    arrays = {
        "wstream": _stream(a),
        "xT": by_channel(a["x"], T),
        "memT": by_channel(a["mem"], TM),
        "params": _params(a),
        "consts": _consts(),
        "rope": _rope(),
        "wsT": np.ascontiguousarray(a["spatial_w_2"].transpose(3, 0, 1, 2)),
        "sbT": np.ascontiguousarray(np.repeat(a["spatial_b_2"].reshape(2, AT, 2, P), HD, axis=2).transpose(2, 0, 1, 3)),
    }
    nc = bacc.Bacc("TRN2", target_bir_lowering=False, num_devices=1)
    aps = {k: nc.dram_tensor(k, v.shape, mybir.dt.from_np(v.dtype), kind="ExternalInput").ap()
           for k, v in arrays.items()}
    out = nc.dram_tensor("out", (P, KT, T), mybir.dt.float32, kind="ExternalOutput").ap()
    two_blocks(nc, out=out, **aps)
    r = run_bass_kernel_spmd(nc, [arrays], core_ids=[0])
    return r.results[0]["out"].transpose(2, 1, 0).reshape(1, T, D)
```
